# Optimizing a Trainium2 kernel written in Bass

```python
import math
import jax, jax.numpy as jnp
from jax import lax
import numpy as np

D_MODEL = 2048
BATCH = 1
SEQ = 256
DEPTH = 1

CHUNK = 64
HEAD_DIM = 64
T5_HEADS = 16
A_HEADS = T5_HEADS
A_KV_HEADS = 2
A_WINDOW_CHUNKS = 2
A_WIDTH = A_HEADS * HEAD_DIM
B_HEADS = T5_HEADS
B_WIDTH = B_HEADS * HEAD_DIM
B_LATENT = 256
IDX_HEADS = 8
IDX_DIM = 64
TOPK_MAX = 256
B_QBLOCK = 128
C_HEADS = 16
C_WIDTH = C_HEADS * HEAD_DIM
C_PREV_CHUNKS = 8
C_REL_MAX = 256
C_REL_SIZE = CHUNK + C_REL_MAX
T5_PAST_BUCKETS = 24
T5_FUT_BUCKETS = 8
T5_BUCKETS = T5_PAST_BUCKETS + T5_FUT_BUCKETS
T5_PAST_EXACT = 12
T5_FUT_EXACT = 4
T5_MAX_DIST = 128
RMS_EPS = 1e-6
NEG = -1e30

PROJ_SIZES = (
    A_WIDTH, A_KV_HEADS * HEAD_DIM, A_KV_HEADS * HEAD_DIM, A_WIDTH,
    B_WIDTH, B_LATENT, IDX_HEADS * IDX_DIM, IDX_DIM, IDX_HEADS, B_WIDTH,
    C_WIDTH, C_WIDTH, C_WIDTH, C_WIDTH,
    D_MODEL, D_MODEL, D_MODEL,
)
PROJ_COLS = sum(PROJ_SIZES)

kernel_name = "hybrid_chunk_causal_swa_dsa_chunkattn"

def _rmsnorm(x, g):
    xf = x.astype(jnp.float32)
    y = xf * lax.rsqrt(jnp.mean(xf * xf, axis=-1, keepdims=True) + RMS_EPS)
    return (y * g.astype(jnp.float32)).astype(x.dtype)

def _split_cols(p):
    offs = np.cumsum(PROJ_SIZES)[:-1].tolist()
    return jnp.split(p, offs, axis=-1)

def _log_bucket(d, n, exact, max_dist):
    d = jnp.maximum(d, 0)
    df = jnp.maximum(d, 1).astype(jnp.float32)
    large = exact + (jnp.log(df / exact) / math.log(max_dist / exact) * (n - exact)).astype(jnp.int32)
    return jnp.where(d < exact, d, jnp.minimum(large, n - 1))

def _t5_bucket(rel):
    past = _log_bucket(-rel, T5_PAST_BUCKETS, T5_PAST_EXACT, T5_MAX_DIST)
    fut = T5_PAST_BUCKETS + _log_bucket(rel - 1, T5_FUT_BUCKETS, T5_FUT_EXACT, CHUNK)
    return jnp.where(rel > 0, fut, past)

def _band_chunks(t):
    parts = []
    for j in range(A_WINDOW_CHUNKS - 1, 0, -1):
        parts.append(jnp.pad(t[:, :-j], ((0, 0), (j, 0)) + ((0, 0),) * (t.ndim - 2)))
    parts.append(t)
    return jnp.concatenate(parts, axis=2)

def _mixer_a(q, k, v, sink, t5_bias):
    b, s = q.shape[:2]
    nc = s // CHUNK
    grp = A_HEADS // A_KV_HEADS
    w = A_WINDOW_CHUNKS * CHUNK
    q = q.reshape(b, nc, CHUNK, A_KV_HEADS, grp, HEAD_DIM)
    kb = _band_chunks(k.reshape(b, nc, CHUNK, A_KV_HEADS, HEAD_DIM))
    vb = _band_chunks(v.reshape(b, nc, CHUNK, A_KV_HEADS, HEAD_DIM))
    logits = jnp.einsum("bnqgrd,bnkgd->bngrqk", q, kb).astype(jnp.float32) * HEAD_DIM ** -0.5
    qi = jnp.arange(CHUNK, dtype=jnp.int32)
    key_off = jnp.arange(w, dtype=jnp.int32) - (A_WINDOW_CHUNKS - 1) * CHUNK
    rel = key_off[None, :] - qi[:, None]
    bias = t5_bias[:, _t5_bucket(rel)].astype(jnp.float32).reshape(A_KV_HEADS, grp, CHUNK, w)
    valid = (jnp.arange(nc, dtype=jnp.int32)[:, None] * CHUNK + key_off[None, :]) >= 0
    logits = jnp.where(valid[None, :, None, None, None, :], logits + bias, NEG)
    sink_l = sink.astype(jnp.float32).reshape(A_KV_HEADS, grp)[None, None, :, :, None, None]
    m = jnp.maximum(jnp.max(logits, axis=-1, keepdims=True), sink_l)
    p = jnp.exp(logits - m)
    probs = p / (jnp.sum(p, axis=-1, keepdims=True) + jnp.exp(sink_l - m))
    out = jnp.einsum("bngrqk,bnkgd->bnqgrd", probs.astype(vb.dtype), vb)
    return out.reshape(b, s, A_WIDTH)

def _mixer_b(q, ckv, iq, ik, iw, w_uk, w_uv, t5_bias):
    b, s = q.shape[:2]
    nb = s // B_QBLOCK
    k_sel = min(TOPK_MAX, s // 4)
    qs = q.reshape(b, nb, B_QBLOCK, B_HEADS, HEAD_DIM).swapaxes(0, 1)
    iqs = iq.reshape(b, nb, B_QBLOCK, IDX_HEADS, IDX_DIM).swapaxes(0, 1)
    iws = iw.reshape(b, nb, B_QBLOCK, IDX_HEADS).swapaxes(0, 1)
    tpos = jnp.arange(s, dtype=jnp.int32).reshape(nb, B_QBLOCK)
    key_chunk = jnp.arange(s, dtype=jnp.int32) // CHUNK

    def block(args):
        qb, iqb, iwb, tb = args
        rel_h = jax.nn.relu(jnp.einsum("bqhd,bsd->bqhs", iqb, ik).astype(jnp.float32) * IDX_DIM ** -0.5)
        score = jnp.einsum("bqh,bqhs->bqs", iwb.astype(jnp.float32), rel_h) * IDX_HEADS ** -0.5
        adm = key_chunk[None, :] <= (tb // CHUNK)[:, None]
        score = jnp.where(adm[None], score, NEG)
        _, idx = lax.top_k(score, k_sel)
        c_sel = jax.vmap(lambda c, i: c[i])(ckv, idx)
        q_lat = jnp.einsum("bqhd,hdc->bqhc", qb, w_uk)
        logits = jnp.einsum("bqhc,bqkc->bhqk", q_lat, c_sel).astype(jnp.float32) * HEAD_DIM ** -0.5
        rel = idx - tb[None, :, None]
        bias = jnp.moveaxis(jnp.take(t5_bias, _t5_bucket(rel), axis=1), 0, 1).astype(jnp.float32)
        valid = (idx // CHUNK) <= (tb // CHUNK)[None, :, None]
        logits = jnp.where(valid[:, None], logits + bias, NEG)
        p = jax.nn.softmax(logits, axis=-1).astype(c_sel.dtype)
        o_lat = jnp.einsum("bhqk,bqkc->bqhc", p, c_sel)
        return jnp.einsum("bqhc,hcd->bqhd", o_lat, w_uv)

    out = lax.map(block, (qs, iqs, iws, tpos))
    return out.swapaxes(0, 1).reshape(b, s, B_WIDTH)

def _mixer_c(q, k, v, rel_table):
    b, s = q.shape[:2]
    nc = s // CHUNK
    pad = C_PREV_CHUNKS * CHUNK
    band = pad + CHUNK
    q = q.reshape(b, s, C_HEADS, HEAD_DIM)
    k_pad = jnp.pad(k.reshape(b, s, C_HEADS, HEAD_DIM), ((0, 0), (pad, 0), (0, 0), (0, 0)))
    v_pad = jnp.pad(v.reshape(b, s, C_HEADS, HEAD_DIM), ((0, 0), (pad, 0), (0, 0), (0, 0)))
    qi = jnp.arange(CHUNK, dtype=jnp.int32)
    ki = jnp.arange(band, dtype=jnp.int32)
    dist = pad + qi[:, None] - ki[None, :]
    bias = rel_table[:, jnp.clip(dist, -(CHUNK - 1), C_REL_MAX) + CHUNK - 1].astype(jnp.float32)

    def chunk(n):
        qn = lax.dynamic_slice_in_dim(q, n * CHUNK, CHUNK, axis=1)
        kn = lax.dynamic_slice_in_dim(k_pad, n * CHUNK, band, axis=1)
        vn = lax.dynamic_slice_in_dim(v_pad, n * CHUNK, band, axis=1)
        logits = jnp.einsum("bqhd,bkhd->bhqk", qn, kn).astype(jnp.float32) * HEAD_DIM ** -0.5 + bias
        valid = n * CHUNK - pad + ki >= 0
        logits = jnp.where(valid, logits, NEG)
        p = jax.nn.softmax(logits, axis=-1).astype(vn.dtype)
        return jnp.einsum("bhqk,bkhd->bqhd", p, vn)

    out = lax.map(chunk, jnp.arange(nc, dtype=jnp.int32))
    return jnp.moveaxis(out, 0, 1).reshape(b, s, C_WIDTH)

def setup_inputs(seed: int = 0) -> dict:
    key = jax.random.key(seed)
    ks = jax.random.split(key, 14)
    f32 = jnp.float32
    nrm = lambda k, shape, scale: jax.random.normal(k, shape, f32) * scale
    return {
        "x": nrm(ks[0], (BATCH, SEQ, D_MODEL), 1.0),
        "ln_g": 1.0 + nrm(ks[1], (DEPTH, D_MODEL), 0.02),
        "w_in": nrm(ks[2], (DEPTH, D_MODEL, PROJ_COLS), D_MODEL ** -0.5),
        "ckv_g": 1.0 + nrm(ks[3], (DEPTH, B_LATENT), 0.02),
        "w_uk": nrm(ks[4], (DEPTH, B_HEADS, HEAD_DIM, B_LATENT), B_LATENT ** -0.5),
        "w_uv": nrm(ks[5], (DEPTH, B_HEADS, B_LATENT, HEAD_DIM), B_LATENT ** -0.5),
        "sink": nrm(ks[6], (DEPTH, A_HEADS), 0.5),
        "c_rel_bias": nrm(ks[7], (DEPTH, C_HEADS, C_REL_SIZE), 0.2),
        "t5_bias": nrm(ks[8], (T5_HEADS, T5_BUCKETS), 0.2),
        "w_pa": nrm(ks[9], (DEPTH, A_WIDTH, D_MODEL), A_WIDTH ** -0.5),
        "w_pb": nrm(ks[10], (DEPTH, B_WIDTH, D_MODEL), B_WIDTH ** -0.5),
        "w_pc": nrm(ks[11], (DEPTH, C_WIDTH, D_MODEL), C_WIDTH ** -0.5),
        "w_o": nrm(ks[12], (DEPTH, D_MODEL, D_MODEL), D_MODEL ** -0.5),
        "final_g": 1.0 + nrm(ks[13], (D_MODEL,), 0.02),
    }

def reference(x, ln_g, w_in, ckv_g, w_uk, w_uv, sink, c_rel_bias, t5_bias, w_pa, w_pb, w_pc, w_o, final_g):
    for l in range(DEPTH):
        h = _rmsnorm(x, ln_g[l])
        (qa, ka, va, za, qb, ckv, iq, ik, iw, zb, qc, kc, vc, zc, ga, gb, gc) = _split_cols(h @ w_in[l])
        ckv = _rmsnorm(ckv, ckv_g[l])
        ya = _mixer_a(qa, ka, va, sink[l], t5_bias) * jax.nn.silu(za)
        yb = _mixer_b(qb, ckv, iq, ik, iw, w_uk[l], w_uv[l], t5_bias) * jax.nn.silu(zb)
        yc = _mixer_c(qc, kc, vc, c_rel_bias[l]) * jax.nn.silu(zc)
        merged = (jax.nn.sigmoid(ga) * (ya @ w_pa[l])
                  + jax.nn.sigmoid(gb) * (yb @ w_pb[l])
                  + jax.nn.sigmoid(gc) * (yc @ w_pc[l]))
        x = x + merged @ w_o[l]
    return _rmsnorm(x, final_g)


_drawn_inputs = setup_inputs


def setup_inputs(seed=0):
    import zlib

    import numpy as np

    out = dict(_drawn_inputs(seed))
    spreads = {}
    factors = {'ln_g': 5.729,
     'ckv_g': 8.0,
     'sink': 8.0,
     'c_rel_bias': 6.318,
     't5_bias': 4.189,
     'final_g': 2.779}
    for name, (base, spread) in spreads.items():
        noise = np.random.default_rng([zlib.crc32(name.encode()), seed]).standard_normal(out[name].shape)
        drawn = base * np.exp(spread * noise) if base else spread * noise
        out[name] = __import__('jax').numpy.asarray(drawn.astype(out[name].dtype))
    for name, factor in factors.items():
        out[name] = (out[name] * factor).astype(out[name].dtype)
    return out
```

```python
import math
from contextlib import ExitStack

import numpy as np
import concourse.bass as bass
from concourse import mybir
from concourse.alu_op_type import AluOpType as ALU

F32 = mybir.dt.float32
F32R = mybir.dt.float32r
ACT = mybir.ActivationFunctionType
ds = bass.ds

P = 128
SEQ, D = 256, 2048
NT = SEQ // P
KT = D // P
HD = 64
BW = 1024
LAT = 256
IH = 8
CH = 512
EPS, NEG = 1e-6, -1e30
TAKEN = -3e38
SROW = 3 * P
TAB = 384

SIZES = dict(qa=1024, ka=128, va=128, za=1024, qb=1024, ckv=256, iq=512, ik=64, iw=8, zb=1024,
             qc=1024, kc=1024, vc=1024, zc=1024, ga=2048, gb=2048, gc=2048)
COL = dict(zip(SIZES, np.cumsum([0] + list(SIZES.values())[:-1]).tolist()))

BR = 10
KINDS = ["q", "q", "i"] + ["q"] * 10 + ["z", "z", "g", "P", "g", "P", "g", "P", "g", "P"] * 3 + ["o"] * 4
PIECES = [8, 8, 4] + [8] * 10 + [8, 8, 8, 4, 8, 4, 8, 4, 8, 4] * 3 + [8] * 4
FIRST = np.cumsum([0] + PIECES).tolist()
NPIECE = FIRST[-1]
LEAD = 2
RING = 4
WARM_UP = 72


class Idx:

    def __init__(self, base, step=0, i=None):
        self.base, self.step, self.i = base, step, i

    def __add__(self, n):
        return Idx(self.base + n, self.step, self.i)

    def of(self, f):
        v = f(self.base)
        return v if self.i is None else v + self.i * (f(self.base + self.step) - v)


def acts_before(c):
    return sum(k in "qi" for k in KINDS[:c])


def dves_before(c):
    return sum(k in "qzP" for k in KINDS[:c])


def tanhs_before(c):
    return 2 * sum(k in "zg" for k in KINDS[:c])


def landed(g):
    q = g // RING + 1
    return 16 * (q + min(q, PIECES[0] // RING))


def bucket(rel):
    f = np.float32

    def log_bucket(d, n, exact, most):
        if d < exact:
            return max(d, 0)
        x = np.log(f(d) / f(exact)) / f(math.log(most / exact)) * f(n - exact)
        return min(exact + int(x), n - 1)

    return 24 + log_bucket(rel - 1, 8, 4, 64) if rel > 0 else log_bucket(-rel, 24, 12, 128)


def runs_of_buckets():
    of = [bucket(127 - m) for m in range(TAB)]
    lo = 0
    for m in range(1, TAB + 1):
        if m == TAB or of[m] != of[lo]:
            yield of[lo], lo, m
            lo = m


def hybrid_trunk(nc, x, ln_g, w_in, ckv_g, w_uk, w_uv, sink, c_rel, t5, w_pa, w_pb, w_pc, w_o, final_g, out):
    table = nc.dram_tensor("bias_table", [48, TAB], F32).ap()

    win_v = w_in[0].rearrange("(k p) n -> p k n", p=P)
    wp_v = [w[0].rearrange("(k p) n -> p k n", p=P) for w in (w_pa, w_pb, w_pc)]
    wo_v = w_o[0].rearrange("(k p) n -> p k n", p=P)
    x_v = x[0].rearrange("(t p) n -> p t n", p=P)
    out_v = out[0].rearrange("(t p) n -> p t n", p=P)
    ZCOL = [COL["za"], COL["zb"], COL["zc"]]
    GCOL = [COL["ga"], COL["gb"], COL["gc"]]

    with ExitStack() as ctx:
        def sb(name, shape, dt=F32):
            return ctx.enter_context(nc.sbuf_tensor(name, shape, dt))

        def sem(name):
            return ctx.enter_context(nc.semaphore(name))

        raw = sb("raw", [P, RING, 1024])
        w_hi = sb("w_hi", [P, RING, 1024], F32R)
        w_lo = sb("w_lo", [P, RING, 1024], F32R)
        h_hi = sb("h_hi", [P, KT, SEQ], F32R)
        h_lo = sb("h_lo", [P, KT, SEQ], F32R)
        y_hi = sb("y_hi", [P, 8, SEQ], F32R)
        y_lo = sb("y_lo", [P, 8, SEQ], F32R)
        act = sb("act", [P, NT, 5 * BW])
        QC, KC, VC = 2 * BW, 3 * BW, 4 * BW
        merged = sb("merged", [P, NT, D])
        k_a = sb("k_a", [P, NT, 4 * P])
        v_a = sb("v_a", [P, NT, 4 * HD])
        k_b = sb("k_b", [P, NT, BW])
        v_b = sb("v_b", [P, NT, BW])
        gate = sb("gate", [P, NT, CH])
        masks = sb("masks", [P, 3, SROW])
        scores = sb("scores", [P, 2, SROW])
        probsT = sb("probsT", [P, 2, SROW])
        qkT = sb("qkT", [P, 4 * P])
        rows = sb("rows", [P, NT, 2 * P])
        bias = sb("bias", [P, 2, 2 * P])
        biasmask = sb("biasmask", [P, 2, SROW])
        work = sb("work", [P, SROW])
        best8 = sb("best8", [P, NT, 8])
        ident = sb("ident", [P, P])
        sinks = sb("sinks", [P, 48])
        neg_sinks = sb("neg_sinks", [P, 48])
        top = sb("top", [P, 2, NT])
        neg_top = sb("neg_top", [P, 2, NT])
        sink_arg = sb("sink_arg", [P, 2, NT])
        sink_exp = sb("sink_exp", [P, 2, NT])
        expsum = sb("expsum", [P, 2, NT])
        denom = sb("denom", [P, 2, NT])
        r_denom = sb("r_denom", [P, 2, NT])
        ssq = sb("ssq", [P, NT])
        ssq_c = sb("ssq_c", [P, NT])
        ssq_o = sb("ssq_o", [P, NT, 4])
        ssq_f = sb("ssq_f", [P, NT])
        mean_sq = sb("mean_sq", [P, 3, NT])
        rstd = sb("rstd", [P, 3, NT])
        fence = sb("fence", [P, 1])
        neg_half = sb("neg_half", [P, NT])
        lng_r = sb("lng_r", [KT, P])
        ln_gT = sb("ln_gT", [P, KT])
        t5_r = sb("t5_r", [16, 32])
        crel_r = sb("crel_r", [16, 320])

        early = merged[:, :, :].rearrange("p a b -> p (a b)")
        ckv = early[:, 0:512].rearrange("p (t c) -> p t c", t=NT)
        ckvT = early[:, 512:1024].rearrange("p (c s) -> p c s", c=2)
        uk = early[:, 1024:1280]
        ukv = early[:, 1280:1792].rearrange("p (c n) -> p c n", c=2)
        ukT = ukv[:, :, 0:P]
        uv = ukv[:, :, P:2 * P].rearrange("p c (h d) -> p c h d", h=2)
        iwT = early[HD:HD + IH, 1792:2048]
        ikT = early[:, 2048:2304]
        iw = early[:, 2304:2320].rearrange("p (t h) -> p t h", t=NT)
        ckvg = early[:, 2320:2576]
        tabs = early[0:16, 2576:2576 + 2 * TAB].rearrange("p (k m) -> p k m", k=2)
        iqT = k_b[:, 0, :].rearrange("p (b s) -> p b s", b=4)
        x_rows = act[:, :, 0:D]
        out_rows = act[:, :, 0:D]
        x_res = act[:, :, KC:KC + D]
        fin_g = k_b[:, :, :].rearrange("p t n -> p (t n)")

        bank = [ctx.enter_context(nc.psum_tensor(f"bank{n}", [P, CH], F32)) for n in range(8)]

        x_in = [sem(f"x_in{t}") for t in range(NT)]
        lng_in = sem("lng_in")
        par_in = sem("par_in")
        sink_in = sem("sink_in")
        ckvg_in = sem("ckvg_in")
        tab_out = sem("tab_out")
        raw_in = [sem(f"raw_in{s}") for s in range(RING)]
        bias_in = sem("bias_in")
        uk_in = sem("uk_in")
        uv_in = sem("uv_in")
        res_in = sem("res_in")
        fing_in = sem("fing_in")
        stored = sem("stored")
        hi_ready = sem("hi_ready")
        lo_ready = sem("lo_ready")
        used = sem("used")
        act_evac = sem("act_evac")
        dve_evac = sem("dve_evac")
        tanh_ready = sem("tanh_ready")
        z_mul = sem("z_mul")
        p_mul = sem("p_mul")
        zeroed = sem("zeroed")
        ident_ready = sem("ident_ready")
        mask_ready = sem("mask_ready")
        selected = sem("selected")
        nsink_ready = sem("nsink_ready")
        tab_ready = sem("tab_ready")
        lngT_ready = sem("lngT_ready")
        lngT_copied = sem("lngT_copied")
        ssq_ready = sem("ssq_ready")
        mean_ready = sem("mean_ready")
        rstd_ready = sem("rstd_ready")
        x_normed = sem("x_normed")
        hT_ready = sem("hT_ready")
        hT_hi = sem("hT_hi")
        hT_lo = sem("hT_lo")
        ckv_normed = sem("ckv_normed")
        ckvT_ready = sem("ckvT_ready")
        ckvT_copied = sem("ckvT_copied")
        iqT_ready = sem("iqT_ready")
        iqT_copied = sem("iqT_copied")
        idx_mm = sem("idx_mm")
        idx_relu = sem("idx_relu")
        idx_acc = sem("idx_acc")
        idx_score = sem("idx_score")
        best_ready = sem("best_ready")
        round_done = sem("round_done")
        ukT_ready = sem("ukT_ready")
        ukT_copied = sem("ukT_copied")
        kv_ready = sem("kv_ready")
        kv_copied = sem("kv_copied")
        rows_ready = sem("rows_ready")
        bm_ready = sem("bm_ready")
        qkT_ready = sem("qkT_ready")
        qkT_copied = sem("qkT_copied")
        scored = sem("scored")
        biased = sem("biased")
        top_ready = sem("top_ready")
        sinkarg_ready = sem("sinkarg_ready")
        exp_ready = sem("exp_ready")
        pT_ready = sem("pT_ready")
        pT0_copied = sem("pT0_copied")
        pT1_copied = sem("pT1_copied")
        pv_ready = sem("pv_ready")
        denom_ready = sem("denom_ready")
        rdenom_ready = sem("rdenom_ready")
        o_ready = sem("o_ready")
        yT_ready = sem("yT_ready")
        yT_hi = sem("yT_hi")
        yT_lo = sem("yT_lo")
        mT_ready = sem("mT_ready")
        mT_hi = sem("mT_hi")
        mT_lo = sem("mT_lo")
        sq_ready = sem("sq_ready")
        sum_ready = sem("sum_ready")
        gained = sem("gained")
        normed = sem("normed")
        normed_1 = sem("normed_1")

        def wait(eng, s, value):
            if not isinstance(value, int) or value > 0:
                eng.wait_ge(s, value)

        def q_cols(br, m):
            return act[:, :, ds(m.of(lambda n: br * BW + P * n), P)]

        def k_cols(br, m):
            if br == 0:
                return k_a[:, :, ds(m.of(lambda n: P * (n // 2)), P)]
            src, off = (k_b, 0) if br == 1 else (act, KC)
            return src[:, :, ds(m.of(lambda n: off + P * n), P)]

        def v_cols(br, m, kt, h):
            if br == 0:
                return v_a[:, kt, ds(m.of(lambda n: HD * (n // 2)), HD)]
            src, off = (v_b, 0) if br == 1 else (act, VC)
            return src[:, kt, ds(m.of(lambda n: off + P * n + HD * h), HD)]

        def pair(br, m):
            return m + 8 * br

        def t_of(t):
            return slice(2 * P, 3 * P) if t == 0 else slice(0, 2 * P)

        block = ctx.enter_context(nc.Block())

        @block.sync
        def _(sp):
            def load(g, src, width=CH, part=0):
                s = g.base % RING
                if part == 0:
                    wait(sp, lo_ready, g.of(lambda n: n - RING + 1))
                kts, w = src.shape[1], src.shape[2]
                slot = raw[:, s, 0:kts * width].rearrange("p (k n) -> p k n", k=kts)
                sp.dma_start(slot[:, :, part:part + w], src).then_inc(raw_in[s], 16)

            def load_chunk(g, view, col, n):
                for j in range(n):
                    load(g + j, view[:, 2 * j:2 * j + 2, ds(col, CH)])

            def load_bias(br, m):
                a = pair(br, m)
                wait(sp, bm_ready, a.of(lambda n: 2 * n))
                t = table[ds(a.of(lambda n: 2 * n), 2), :]
                src = bass.AP(tensor=t.tensor, offset=t.offset, ap=[[1, P], [TAB, 2], [1, 2 * P]])
                sp.dma_start(bias[:, :, :], src).then_inc(bias_in, 16)

            def load_uk_uv(m):
                wait(sp, ukT_ready, m.of(lambda n: n))
                wk = w_uk[0, ds(m.of(lambda n: 2 * n), 2), :, :]
                sp.dma_start(uk, wk.rearrange("h d c -> (h d) c")).then_inc(uk_in, 16)
                wait(sp, kv_ready, m.of(lambda n: n))
                wv = w_uv[0, ds(m.of(lambda n: 2 * n), 2), :, :].rearrange("h (c p) d -> p c h d", p=P)
                for c in range(2):
                    sp.dma_start(uv[:, c, :, :], wv[:, c, :, :]).then_inc(uv_in, 16)

            for t in range(NT):
                sp.dma_start(x_rows[:, t, :], x_v[:, t, :]).then_inc(x_in[t], 16)
            for j in range(8):
                load(Idx(j), win_v[:, 2 * j:2 * j + 2, COL["ka"]:COL["ka"] + 256], part=0)
                load(Idx(j), win_v[:, 2 * j:2 * j + 2, COL["ckv"]:COL["ckv"] + 256], part=256)
            load_chunk(Idx(FIRST[1]), win_v, COL["iq"], 8)
            for j in range(4):
                load(Idx(FIRST[2] + j), win_v[:, 4 * j:4 * j + 4, COL["ik"]:COL["ik"] + 72], width=72)
            for n in range(2):
                load_chunk(Idx(FIRST[3 + n]), win_v, COL["qa"] + CH * n, 8)
            sp.wait_ge(tab_out, 48)

            def load_for_pair_a(m, g, col):
                for j in range(8):
                    load(g + j, win_v[:, 2 * j:2 * j + 2, ds(col, CH)])
                    if j == 1:
                        load_uk_uv(m)
                    if j == 2:
                        load_bias(0, m)

            for u in range(2):
                load_for_pair_a(Idx(u), Idx(FIRST[5 + u]), COL["qb"] + CH * u)
            with sp.Fori(0, 3) as i:
                for u in range(2):
                    load_for_pair_a(Idx(2 + u, 2, i), Idx(FIRST[7 + u], 16, i),
                                    i * (2 * CH) + (COL["qc"] + CH * u))
            for b in range(3):
                g0 = FIRST[13 + BR * b]
                for u in range(2):
                    if b < 2:
                        load_bias(b + 1, Idx(u))
                    load_chunk(Idx(g0 + 8 * u), win_v, ZCOL[b] + CH * u, 8)
                load_chunk(Idx(g0 + 16), win_v, GCOL[b], 8)
                if b == 2:
                    sp.wait_ge(pv_ready, 24)
                    sp.dma_start(x_res, x_v).then_inc(res_in, 16)
                    sp.dma_start(fin_g, final_g.rearrange("(a n) -> a n", a=1).to_broadcast([P, D])
                                 ).then_inc(fing_in, 16)
                with sp.Fori(0, 3) as i:
                    g = Idx(g0 + 24, 12, i)
                    for j in range(4):
                        load(g + j, wp_v[b][:, 2 * j:2 * j + 2, ds(i * CH, CH)])
                        if j == 1 and b < 2:
                            load_bias(b + 1, Idx(2, 2, i))
                    for j in range(8):
                        load(g + (4 + j), win_v[:, 2 * j:2 * j + 2, ds(i * CH + (GCOL[b] + CH), CH)])
                        if j == 3 and b < 2:
                            load_bias(b + 1, Idx(3, 2, i))
                for j in range(4):
                    load(Idx(g0 + 60 + j), wp_v[b][:, 2 * j:2 * j + 2, 3 * CH:4 * CH])
            with sp.Fori(0, 4) as i:
                for j in range(8):
                    load(Idx(FIRST[43] + j, 8, i), wo_v[:, 2 * j:2 * j + 2, ds(i * CH, CH)])
            for t, half, s, n in ((0, 0, normed, 1), (1, 0, normed_1, 1), (0, 1, normed, 2), (1, 1, normed, 3)):
                cols = slice(D // 2 * half, D // 2 * (half + 1))
                sp.wait_ge(s, n)
                sp.dma_start(out_v[:, t, cols], x_res[:, t, cols]).then_inc(stored, 16)
            sp.wait_ge(stored, 16 * 4)

        @block.gpsimd
        def _(pool):
            def rms(n, src, width, count):
                pool.wait_ge(ssq_ready, count)
                nc.gpsimd.tensor_scalar(mean_sq[:, n, :], src, 1.0 / width, EPS, ALU.mult, ALU.add
                                        ).then_inc(mean_ready, 1)
                pool.wait_ge(mean_ready, n + 1)
                nc.gpsimd.tensor_tensor(rstd[:, n, :], mean_sq[:, n, :], neg_half[:, :], ALU.pow
                                        ).then_inc(rstd_ready, 1)

            def stage(br, m):
                a = pair(br, m)
                wait(pool, qkT_ready, a.of(lambda n: n))
                nc.gpsimd.tensor_copy(rows[:, :, 0:P], q_cols(br, m)).then_inc(rows_ready, 1)
                nc.gpsimd.tensor_copy(rows[:, :, P:2 * P], k_cols(br, m)).then_inc(rows_ready, 1)
                wait(pool, biased, a.of(lambda n: 4 * n))
                pool.wait_ge(bias_in, a.of(lambda n: 16 * n + 16))
                for t in (1, 0):
                    cols = t_of(t)
                    w = cols.stop - cols.start
                    nc.gpsimd.tensor_tensor(
                        biasmask[:, :, cols], bias[:, :, w - 1::-1],
                        masks[:, br:br + 1, cols].to_broadcast([P, 2, w]), ALU.add).then_inc(bm_ready, 1)

            pool.dma_start(lng_r[:, :], ln_g[0].rearrange("(k p) -> k p", p=P)).then_inc(lng_in, 16)
            nc.gpsimd.memset(ident[:, :], 0.0).then_inc(zeroed, 1)
            nc.gpsimd.memset(masks[:, :, :], 0.0).then_inc(zeroed, 1)
            nc.gpsimd.memset(sinks[:, 16:48], NEG).then_inc(zeroed, 1)
            nc.gpsimd.memset(neg_half[:, :], -0.5).then_inc(zeroed, 1)
            pool.wait_ge(zeroed, 4)
            nc.gpsimd.affine_select(out=ident[:, :], in_=ident[:, :], compare_op=ALU.not_equal, fill=1.0,
                                    base=0, pattern=[[-1, P]], channel_multiplier=1).then_inc(ident_ready, 1)
            for br in (0, 2):
                nc.gpsimd.memset(masks[0:HD, br, 3 * HD:4 * HD], NEG).then_inc(mask_ready, 1)
                nc.gpsimd.memset(masks[0:HD, br, 5 * HD:6 * HD], NEG).then_inc(mask_ready, 1)
            nc.gpsimd.memset(masks[0:HD, 0, 0:HD], NEG).then_inc(mask_ready, 1)
            pool.wait_ge(ident_ready, 1)
            pool.wait_ge(mask_ready, 5)
            nc.gpsimd.memset(masks[HD:P, 0, 0:2 * HD], NEG).then_inc(mask_ready, 1)
            pool.wait_ge(mask_ready, 6)

            pool.dma_start(t5_r[:, :], t5).then_inc(par_in, 16)
            pool.dma_start(crel_r[:, :], c_rel[0]).then_inc(par_in, 16)
            pool.dma_start(sinks[:, 0:16], sink.to_broadcast([P, 16])).then_inc(sink_in, 16)
            pool.dma_start(ckvg, ckv_g.to_broadcast([P, LAT])).then_inc(ckvg_in, 16)

            rms(0, ssq[:, :], D, 2)
            pool.wait_ge(tab_ready, len(list(runs_of_buckets())) + 2)
            for n, which in enumerate((0, 0, 1)):
                pool.dma_start(table[16 * n:16 * n + 16, :], tabs[:, which, :]).then_inc(tab_out, 16)
            rms(1, ssq_c[:, :], LAT, 4)
            pool.wait_ge(act_evac, acts_before(5))
            pool.wait_ge(dve_evac, dves_before(5))
            for u in range(2):
                stage(0, Idx(u))
            with pool.Fori(0, 3) as i:
                for u in range(2):
                    stage(0, Idx(2 + u, 2, i))
            pool.wait_ge(kv_copied, 16)
            pool.wait_ge(act_evac, acts_before(13))
            pool.wait_ge(dve_evac, dves_before(13))
            pool.wait_ge(selected, 1)
            for br in (1, 2):
                for u in range(2):
                    stage(br, Idx(u))
                with pool.Fori(0, 3) as i:
                    for u in range(2):
                        stage(br, Idx(2 + u, 2, i))
            rms(2, ssq_f[:, :], D, 5)

        @block.scalar
        def _(sc):
            def hi(g):
                if g.base >= NPIECE:
                    return
                s = g.base % RING
                n = 288 if FIRST[2] <= g.base < FIRST[3] else 1024
                sc.wait_ge(raw_in[s], g.of(landed))
                wait(sc, used, g.of(lambda v: v - RING + 1))
                nc.scalar.activation(w_hi[:, s, 0:n], raw[:, s, 0:n], ACT.Copy).then_inc(hi_ready, 1)

            def attend(k, a):
                if k == 1:
                    sc.wait_ge(qkT_ready, a.of(lambda n: n + 1))
                    nc.scalar.activation(qkT[:, 0:2 * P], bank[7][:, 0:2 * P], ACT.Copy, scale=HD ** -0.5
                                         ).then_inc(qkT_copied, 1)
                    nc.scalar.activation(qkT[:, 2 * P:], bank[7][:, 2 * P:], ACT.Copy).then_inc(qkT_copied, 1)
                if k == 3:
                    sc.wait_ge(top_ready, a.of(lambda n: n + 1))
                    for h in range(2):
                        for t in (1, 0):
                            s = scores[:, h, t_of(t)]
                            nc.scalar.activation(s, s, ACT.Exp, bias=neg_top[:, h, t:t + 1],
                                                 accum_out=expsum[:, h, t:t + 1]).then_inc(exp_ready, 1)
                    sc.wait_ge(sinkarg_ready, a.of(lambda n: n + 1))
                    nc.scalar.activation(sink_exp[:, :, :], sink_arg[:, :, :], ACT.Exp).then_inc(exp_ready, 1)
                if k == 5:
                    sc.wait_ge(pT_ready, a.of(lambda n: 2 * n + 2))
                    nc.scalar.activation(probsT[:, 1, :], bank[7][:, 0:SROW], ACT.Copy).then_inc(pT1_copied, 1)

            def transpose_hi(count, src, dst, ready, done):
                sc.wait_ge(ready, count)
                nc.scalar.activation(dst, src, ACT.Copy).then_inc(done, 1)

            for t in range(NT):
                sc.wait_ge(x_in[t], 16)
                nc.scalar.activation(act[:, t, KC:KC + D], x_rows[:, t, :], ACT.Square,
                                     accum_out=ssq[:, t:t + 1]).then_inc(ssq_ready, 1)
            hi(Idx(0))
            sc.wait_ge(lngT_ready, 1)
            nc.scalar.copy(ln_gT[:, :], bank[0][:, 0:KT]).then_inc(lngT_copied, 1)

            def hT_group(k):
                sc.wait_ge(hT_ready, k + 1)
                sc.wait_ge(lngT_copied, 1)
                for e in range(2):
                    kt = 2 * k + e
                    nc.scalar.activation(h_hi[:, kt, :], bank[4 + k % 4][:, e * SEQ:(e + 1) * SEQ], ACT.Copy,
                                         scale=ln_gT[:, kt:kt + 1]).then_inc(hT_hi, 1)

            hT_group(0)
            hT_group(1)
            hi(Idx(1))
            hT_group(2)
            hT_group(3)

            for j in range(8):
                hi(Idx(j + LEAD))
                if j < 4:
                    hT_group(4 + j)
            sc.wait_ge(used, FIRST[1])
            nc.scalar.copy(k_a[:, 0, :].rearrange("p (g r d) -> p g r d", g=2, r=4),
                           bank[0][:, 0:128].rearrange("p (g d) -> p g d", g=2).unsqueeze(2)
                           .to_broadcast([P, 2, 4, HD]))
            nc.scalar.copy(v_a[:, 0, :].rearrange("p (g r d) -> p g r d", g=2, r=2),
                           bank[0][:, 128:256].rearrange("p (g d) -> p g d", g=2).unsqueeze(2)
                           .to_broadcast([P, 2, 2, HD]))
            nc.scalar.copy(ckv[:, 0, :], bank[0][:, 256:512]).then_inc(act_evac, 1)
            for j in range(8):
                hi(Idx(FIRST[1] + j + LEAD))
                if j == 1:
                    sc.wait_ge(act_evac, 1)
                    sc.wait_ge(dve_evac, 1)
                    for t in range(NT):
                        nc.scalar.activation(act[:, t, KC:KC + LAT], ckv[:, t, :], ACT.Square,
                                             accum_out=ssq_c[:, t:t + 1]).then_inc(ssq_ready, 1)
                if j == 5:
                    sc.wait_ge(ckvT_ready, 1)
                    nc.scalar.copy(ckvT, bank[7][:, :].rearrange("p (c s) -> p c s", c=2)).then_inc(ckvT_copied, 1)
            sc.wait_ge(used, FIRST[2])
            nc.scalar.copy(v_b[:, 0, 0:CH], bank[2][:, :]).then_inc(act_evac, 1)
            for j in range(4):
                hi(Idx(FIRST[2] + j + LEAD))
            sc.wait_ge(used, FIRST[3])
            nc.scalar.copy(ikT[0:HD, :], bank[0][0:HD, 0:SEQ])
            nc.scalar.copy(ikT[HD:P, :], bank[0][0:HD, 0:SEQ])
            nc.scalar.copy(iwT, bank[0][HD:HD + IH, 0:SEQ]).then_inc(act_evac, 1)
            for j in range(8):
                hi(Idx(FIRST[3] + j + LEAD))
                if j == 2:
                    for k in range(2):
                        sc.wait_ge(iqT_ready, k + 1)
                        nc.scalar.copy(iqT[:, 2 * k:2 * k + 2, :],
                                       bank[4 + k][:, :].rearrange("p (b s) -> p b s", b=2)).then_inc(iqT_copied, 1)
                    sc.wait_ge(iqT_ready, 3)
                    nc.scalar.copy(iw, bank[6][:, 0:NT * IH].rearrange("p (t h) -> p t h", t=NT)
                                   ).then_inc(iqT_copied, 1)
                if 4 <= j <= 7:
                    for h in (2 * (j - 4), 2 * (j - 4) + 1):
                        sc.wait_ge(idx_mm, h + 1)
                        wait(sc, idx_acc, 2 * (h - 1))
                        nc.scalar.activation(scores[:, h % 2, :], bank[4 + h % 4][:, 0:SROW], ACT.Relu,
                                             scale=HD ** -0.5).then_inc(idx_relu, 1)
            sc.wait_ge(used, FIRST[4])
            nc.scalar.copy(act[:, 0, 0:CH], bank[2][:, :]).then_inc(act_evac, 1)
            for j in range(8):
                hi(Idx(FIRST[4] + j + LEAD))
            sc.wait_ge(used, FIRST[5])
            nc.scalar.copy(act[:, 0, CH:2 * CH], bank[0][:, :]).then_inc(act_evac, 1)


            def pair_a_chunk(m, g, c):
                for j in range(8):
                    hi(g + (j + LEAD))
                    attend(j - 1, m)
                    if j == 4:
                        sc.wait_ge(kv_ready, m.of(lambda n: n + 1))
                        for half, dst in enumerate((k_b, v_b)):
                            nc.scalar.copy(dst[:, :, ds(m.of(lambda n: P * n), P)],
                                           bank[7][:, :].rearrange("p (t w) -> p t w", t=NT)[
                                               :, :, half * P:(half + 1) * P]).then_inc(kv_copied, 1)
                sc.wait_ge(used, (g + 8).of(lambda n: n))
                nc.scalar.copy(act[:, 0, ds(m.of(lambda n: BW + CH * n), CH)], bank[2 * (c.base % 2)][:, :]
                               ).then_inc(act_evac, 1)

            for u in range(2):
                pair_a_chunk(Idx(u), Idx(FIRST[5 + u]), Idx(5 + u))
            with sc.Fori(0, 3) as i:
                for u in range(2):
                    pair_a_chunk(Idx(2 + u, 2, i), Idx(FIRST[7 + u], 16, i), Idx(7 + u, 2, i))

            def tanh_chunk(c, g_end):
                sc.wait_ge(used, g_end.of(lambda n: n))
                sc.wait_ge(dve_evac, c.of(dves_before))
                b0 = 2 * (c.base % 2)
                for t in range(NT):
                    nc.scalar.activation(gate[:, t, :], bank[b0 + t][:, :], ACT.Tanh, scale=0.5
                                         ).then_inc(tanh_ready, 1)

            for b in range(3):
                c0, g0 = 13 + BR * b, FIRST[13 + BR * b]
                for u in range(2):
                    for j in range(8):
                        hi(Idx(g0 + 8 * u + j + LEAD))
                        if b < 2:
                            attend(j - 1, pair(b + 1, Idx(u)))
                    tanh_chunk(Idx(c0 + u), Idx(g0 + 8 * u + 8))
                for j in range(8):
                    hi(Idx(g0 + 16 + j + LEAD))
                    if 2 <= j <= 5:
                        k = j - 2
                        transpose_hi(4 * b + k + 1, bank[4 + k][:, :].rearrange("p (c s) -> p c s", c=2),
                                     y_hi[:, 2 * k:2 * k + 2, :], yT_ready, yT_hi)
                tanh_chunk(Idx(c0 + 2), Idx(g0 + 24))
                with sc.Fori(0, 3) as i:
                    for j in range(12):
                        hi(Idx(g0 + 24 + j + LEAD, 12, i))
                        if b < 2:
                            attend(j, pair(b + 1, Idx(2, 2, i)))
                            attend(j - 5, pair(b + 1, Idx(3, 2, i)))
                    tanh_chunk(Idx(c0 + 4, 2, i), Idx(g0 + 36, 12, i))
                for j in range(4):
                    hi(Idx(g0 + 60 + j + LEAD))
                    if b == 2 and j >= 1:
                        for e in range(2):
                            n = 2 * (j - 1) + e
                            transpose_hi(n + 1, bank[4 + n % 4][:, :].rearrange("p (c s) -> p c s", c=2),
                                         h_hi[:, 2 * n:2 * n + 2, :], mT_ready, mT_hi)
            for n in range(4):
                for j in range(8):
                    hi(Idx(FIRST[43 + n] + j + LEAD))
                    if n == 0 and j == 2:
                        for k in (6, 7):
                            transpose_hi(k + 1, bank[4 + k % 4][:, :].rearrange("p (c s) -> p c s", c=2),
                                         h_hi[:, 2 * k:2 * k + 2, :], mT_ready, mT_hi)
                    if n > 0 and j == 2:
                        for t in range(NT):
                            sc.wait_ge(sum_ready, NT * (n - 1) + t + 1)
                            nc.scalar.activation(gate[:, t, :], out_rows[:, t, CH * (n - 1):CH * n], ACT.Square,
                                                 accum_out=ssq_o[:, t, n - 1:n]).then_inc(sq_ready, 1)
            for t in range(NT):
                sc.wait_ge(sum_ready, NT * 3 + t + 1)
                nc.scalar.activation(gate[:, t, :], out_rows[:, t, CH * 3:CH * 4], ACT.Square,
                                     accum_out=ssq_o[:, t, 3:4]).then_inc(sq_ready, 1)
            sc.wait_ge(gained, NT * 4)
            sc.wait_ge(rstd_ready, 3)
            nc.scalar.activation(x_res[:, 1, 0:D // 2], x_res[:, 1, 0:D // 2], ACT.Copy, scale=rstd[:, 2, 1:2]
                                 ).then_inc(normed_1, 1)

        @block.vector
        def _(ve):
            def lo(g):
                if g.base >= NPIECE:
                    return
                s = g.base % RING
                n = 288 if FIRST[2] <= g.base < FIRST[3] else 1024
                ve.wait_ge(hi_ready, g.of(lambda v: v + 1))
                nc.vector.tensor_tensor(w_lo[:, s, 0:n], raw[:, s, 0:n], w_hi[:, s, 0:n].bitcast(F32),
                                        ALU.subtract).then_inc(lo_ready, 1)

            def attend(k, a, br, m):
                if k == 2:
                    ve.wait_ge(bm_ready, a.of(lambda n: 2 * n + 2))
                    ve.wait_ge(scored, a.of(lambda n: n + 1))
                    nc.vector.memset(fence[:, :], 0.0)
                    for h in range(2):
                        for t in (1, 0):
                            nc.vector.tensor_tensor_reduce(
                                out=scores[:, h, t_of(t)], in0=bank[4 + h][:, t_of(t)],
                                in1=biasmask[:, h, t_of(t)], scale=1.0, scalar=-3.4e38, op0=ALU.add,
                                op1=ALU.max, accum_out=top[:, h, t:t + 1]).then_inc(biased, 1)
                    s_cols = ds(a.of(lambda n: 2 * n), 2)
                    ve.wait_ge(biased, a.of(lambda n: 4 * n + 4))
                    nc.vector.scalar_tensor_tensor(
                        neg_top[:, :, :], top[:, :, :], -1.0,
                        neg_sinks[:, s_cols].unsqueeze(2).to_broadcast([P, 2, NT]), ALU.mult, ALU.min
                    ).then_inc(top_ready, 1)
                    ve.wait_ge(top_ready, a.of(lambda n: n + 1))
                    nc.vector.tensor_tensor(
                        sink_arg[:, :, :], neg_top[:, :, :],
                        sinks[:, s_cols].unsqueeze(2).to_broadcast([P, 2, NT]), ALU.add
                    ).then_inc(sinkarg_ready, 1)
                if k == 5:
                    ve.wait_ge(pT_ready, a.of(lambda n: 2 * n + 1))
                    nc.vector.tensor_copy(probsT[:, 0, :], bank[6][:, 0:SROW]).then_inc(pT0_copied, 1)
                if k == 6:
                    ve.wait_ge(exp_ready, a.of(lambda n: 5 * n + 5))
                    nc.vector.tensor_tensor(denom[:, :, :], expsum[:, :, :], sink_exp[:, :, :], ALU.add
                                            ).then_inc(denom_ready, 1)
                    ve.wait_ge(denom_ready, a.of(lambda n: n + 1))
                    nc.vector.reciprocal(r_denom[:, :, :], denom[:, :, :]).then_inc(rdenom_ready, 1)
                    ve.wait_ge(rdenom_ready, a.of(lambda n: n + 1))
                    ve.wait_ge(pv_ready, a.of(lambda n: n + 1))
                    nc.vector.tensor_tensor(
                        q_cols(br, m).rearrange("p t (h d) -> p t h d", h=2),
                        bank[4][:, 0:256].rearrange("p (t h d) -> p t h d", t=NT, h=2),
                        r_denom[:, :, :].rearrange("p h t -> p t h").unsqueeze(3).to_broadcast([P, NT, 2, HD]),
                        ALU.mult).then_inc(o_ready, 1)

            def transpose_lo(count, src, dst_hi, dst, hi_done, done):
                ve.wait_ge(hi_done, count)
                nc.vector.tensor_tensor(dst, src, dst_hi.bitcast(F32), ALU.subtract).then_inc(done, 1)

            def scale_x(n):
                for t in range(NT):
                    q = x_rows[:, t, CH * n:CH * (n + 1)]
                    nc.vector.tensor_scalar(q, q, rstd[:, 0, t:t + 1], None, ALU.mult).then_inc(x_normed, 1)

            def hT_group(k):
                for e in range(2):
                    kt = 2 * k + e
                    ve.wait_ge(hT_hi, 2 * k + 2)
                    nc.vector.scalar_tensor_tensor(
                        h_lo[:, kt, :], bank[4 + k % 4][:, e * SEQ:(e + 1) * SEQ], ln_gT[:, kt:kt + 1],
                        h_hi[:, kt, :].bitcast(F32), ALU.mult, ALU.subtract).then_inc(hT_lo, 1)

            ve.wait_ge(rstd_ready, 1)
            scale_x(0)
            lo(Idx(0))
            hT_group(0)
            scale_x(1)
            hT_group(1)
            lo(Idx(1))
            scale_x(2)
            hT_group(2)
            scale_x(3)
            hT_group(3)
            for j in range(8):
                lo(Idx(j + LEAD))
                if j < 4:
                    hT_group(4 + j)
            ve.wait_ge(par_in, 32)
            for b, lo_m, hi_m in runs_of_buckets():
                nc.vector.tensor_copy(tabs[:, 0, lo_m:hi_m], t5_r[:, b:b + 1].to_broadcast([16, hi_m - lo_m])
                                      ).then_inc(tab_ready, 1)
            nc.vector.tensor_copy(tabs[:, 1, HD:TAB], crel_r[:, :]).then_inc(tab_ready, 1)
            nc.vector.tensor_copy(tabs[:, 1, 0:HD], crel_r[:, 0:1].to_broadcast([16, HD])).then_inc(tab_ready, 1)
            ve.wait_ge(sink_in, 16)
            ve.wait_ge(zeroed, 4)
            nc.vector.tensor_scalar(neg_sinks[:, :], sinks[:, :], -1.0, None, ALU.mult).then_inc(nsink_ready, 1)
            ve.wait_ge(used, FIRST[1])
            nc.vector.tensor_copy(k_a[:, 1, :].rearrange("p (g r d) -> p g r d", g=2, r=4),
                                  bank[1][:, 0:128].rearrange("p (g d) -> p g d", g=2).unsqueeze(2)
                                  .to_broadcast([P, 2, 4, HD]))
            nc.vector.tensor_copy(v_a[:, 1, :].rearrange("p (g r d) -> p g r d", g=2, r=2),
                                  bank[1][:, 128:256].rearrange("p (g d) -> p g d", g=2).unsqueeze(2)
                                  .to_broadcast([P, 2, 2, HD]))
            nc.vector.tensor_copy(ckv[:, 1, :], bank[1][:, 256:512]).then_inc(dve_evac, 1)
            for j in range(8):
                lo(Idx(FIRST[1] + j + LEAD))
                if j == 3:
                    ve.wait_ge(rstd_ready, 2)
                    ve.wait_ge(ckvg_in, 16)
                    for t in range(NT):
                        nc.vector.scalar_tensor_tensor(ckv[:, t, :], ckv[:, t, :], rstd[:, 1, t:t + 1], ckvg,
                                                       ALU.mult, ALU.mult).then_inc(ckv_normed, 1)
            ve.wait_ge(used, FIRST[2])
            nc.vector.tensor_copy(v_b[:, 1, 0:CH], bank[3][:, :]).then_inc(dve_evac, 1)
            for j in range(4):
                lo(Idx(FIRST[2] + j + LEAD))
            for j in range(8):
                lo(Idx(FIRST[3] + j + LEAD))
                if 4 <= j <= 7:
                    for h in (2 * (j - 4), 2 * (j - 4) + 1):
                        ve.wait_ge(iqT_copied, 3)
                        ve.wait_ge(idx_relu, h + 1)
                        wait(ve, idx_acc, 2 * h)
                        for t in (1, 0):
                            w, cols = iw[:, t, h:h + 1], t_of(t)
                            if h == 0:
                                ins = nc.vector.tensor_scalar(work[:, cols], scores[:, 0, cols], w, None, ALU.mult)
                            else:
                                ins = nc.vector.scalar_tensor_tensor(work[:, cols], scores[:, h % 2, cols], w,
                                                                     work[:, cols], ALU.mult, ALU.add)
                            ins.then_inc(idx_acc, 1)
            ve.wait_ge(used, FIRST[4])
            nc.vector.tensor_copy(act[:, 1, 0:CH], bank[3][:, :]).then_inc(dve_evac, 1)
            for j in range(8):
                lo(Idx(FIRST[4] + j + LEAD))
                if j == 0:
                    ve.wait_ge(idx_acc, 2 * IH)
                    ve.wait_ge(mask_ready, 6)
                    nc.vector.scalar_tensor_tensor(work[:, :], work[:, :], IH ** -0.5, masks[:, 2, :],
                                                   ALU.mult, ALU.add).then_inc(idx_score, 1)
            ve.wait_ge(used, FIRST[5])
            nc.vector.tensor_copy(act[:, 1, CH:2 * CH], bank[1][:, :]).then_inc(dve_evac, 1)
            ve.wait_ge(idx_score, 1)
            ve.wait_ge(nsink_ready, 1)

            def pair_a_chunk(m, g, c):
                for j in range(8):
                    lo(g + (j + LEAD))
                    if j == 1:
                        ve.wait_ge(ukT_ready, m.of(lambda n: n + 1))
                        nc.vector.tensor_copy(ukT, bank[6][:, 0:256].rearrange("p (c n) -> p c n", c=2)
                                              ).then_inc(ukT_copied, 1)
                    if j == 4:
                        ve.wait_ge(idx_score, 1)
                        wait(ve, round_done, m.of(lambda n: 2 * n))
                        nc.vector.memset(fence[:, :], 0.0)
                        for t in (1, 0):
                            nc.vector.max(best8[:, t, :], work[:, t_of(t)]).then_inc(best_ready, 1)
                        ve.wait_ge(best_ready, m.of(lambda n: 2 * n + 2))
                        nc.vector.memset(fence[:, :], 0.0)
                        for t in (1, 0):
                            nc.vector.match_replace(work[:, t_of(t)], best8[:, t, :], work[:, t_of(t)], TAKEN
                                                    ).then_inc(round_done, 1)
                    attend(j - 1, m, 0, m)
                ve.wait_ge(used, (g + 8).of(lambda n: n))
                nc.vector.tensor_copy(act[:, 1, ds(m.of(lambda n: BW + CH * n), CH)],
                                      bank[2 * (c.base % 2) + 1][:, :]).then_inc(dve_evac, 1)

            for u in range(2):
                pair_a_chunk(Idx(u), Idx(FIRST[5 + u]), Idx(5 + u))
            with ve.Fori(0, 3) as i:
                for u in range(2):
                    pair_a_chunk(Idx(2 + u, 2, i), Idx(FIRST[7 + u], 16, i), Idx(7 + u, 2, i))
            ve.wait_ge(round_done, 16)
            nc.vector.tensor_scalar(masks[:, 1, :], work[:, :], TAKEN / 2, NEG, ALU.is_ge, ALU.mult
                                    ).then_inc(selected, 1)

            def silu_chunk(b, u):
                c = 13 + BR * b + u
                n0 = 2 * (2 * b + u)
                for t in range(NT):
                    ve.wait_ge(tanh_ready, tanhs_before(c) + t + 1)
                    nc.vector.scalar_tensor_tensor(gate[:, t, :], gate[:, t, :], 1.0, bank[2 * (c % 2) + t][:, :],
                                                   ALU.add, ALU.mult).then_inc(z_mul, 1)
                for t in range(NT):
                    ve.wait_ge(z_mul, n0 + t + 1)
                    o = act[:, t, BW * b + CH * u:BW * b + CH * (u + 1)]
                    ins = nc.vector.scalar_tensor_tensor(o, gate[:, t, :], 0.25, o, ALU.mult, ALU.mult)
                ins.then_inc(dve_evac, 1)

            def merge_chunk(b, c, n, g_end):
                ve.wait_ge(used, g_end.of(lambda v: v))
                ve.wait_ge(tanh_ready, c.of(tanhs_before))
                b0 = 2 * (c.base % 2)
                for t in range(NT):
                    dst = merged[:, t, ds(n.of(lambda v: CH * v), CH)]
                    if b == 0:
                        ins = nc.vector.scalar_tensor_tensor(dst, gate[:, t, :], 1.0, bank[b0 + t][:, :],
                                                             ALU.add, ALU.mult)
                    else:
                        nc.vector.scalar_tensor_tensor(gate[:, t, :], gate[:, t, :], 1.0, bank[b0 + t][:, :],
                                                       ALU.add, ALU.mult).then_inc(p_mul, 1)
                if b > 0:
                    for t in range(NT):
                        ve.wait_ge(p_mul, n.of(lambda v: 8 * (b - 1) + 2 * v + t + 1))
                        dst = merged[:, t, ds(n.of(lambda v: CH * v), CH)]
                        ins = nc.vector.tensor_tensor(dst, dst, gate[:, t, :], ALU.add)
                ins.then_inc(dve_evac, 1)

            for b in range(3):
                c0, g0 = 13 + BR * b, FIRST[13 + BR * b]
                for u in range(2):
                    for j in range(8):
                        lo(Idx(g0 + 8 * u + j + LEAD))
                        if b < 2:
                            attend(j - 1, pair(b + 1, Idx(u)), b + 1, Idx(u))
                    silu_chunk(b, u)
                for j in range(8):
                    lo(Idx(g0 + 16 + j + LEAD))
                    if 2 <= j <= 5:
                        k = j - 2
                        transpose_lo(4 * b + k + 1, bank[4 + k][:, :].rearrange("p (c s) -> p c s", c=2),
                                     y_hi[:, 2 * k:2 * k + 2, :], y_lo[:, 2 * k:2 * k + 2, :], yT_hi, yT_lo)
                with ve.Fori(0, 3) as i:
                    for j in range(12):
                        lo(Idx(g0 + 24 + j + LEAD, 12, i))
                        if j == 4:
                            merge_chunk(b, Idx(c0 + 3, 2, i), Idx(0, 1, i), Idx(g0 + 28, 12, i))
                        if b < 2:
                            for m, p0 in ((Idx(2, 2, i), 0), (Idx(3, 2, i), 5)):
                                attend(j - p0, pair(b + 1, m), b + 1, m)
                for j in range(4):
                    lo(Idx(g0 + 60 + j + LEAD))
                    if b == 2 and j >= 1:
                        for e in range(2):
                            n = 2 * (j - 1) + e
                            transpose_lo(n + 1, bank[4 + n % 4][:, :].rearrange("p (c s) -> p c s", c=2),
                                         h_hi[:, 2 * n:2 * n + 2, :], h_lo[:, 2 * n:2 * n + 2, :], mT_hi, mT_lo)
                merge_chunk(b, Idx(c0 + 9), Idx(3), Idx(g0 + 64))
            for n in range(4):
                for j in range(8):
                    lo(Idx(FIRST[43 + n] + j + LEAD))
                    if n == 0 and j == 2:
                        for k in (6, 7):
                            transpose_lo(k + 1, bank[4 + k % 4][:, :].rearrange("p (c s) -> p c s", c=2),
                                         h_hi[:, 2 * k:2 * k + 2, :], h_lo[:, 2 * k:2 * k + 2, :], mT_hi, mT_lo)
                ve.wait_ge(used, FIRST[43 + n] + 8)
                ve.wait_ge(res_in, 16)
                for t in range(NT):
                    cols = slice(CH * n, CH * (n + 1))
                    nc.vector.tensor_tensor(out_rows[:, t, cols], bank[2 * ((43 + n) % 2) + t][:, :],
                                            x_res[:, t, cols], ALU.add).then_inc(sum_ready, 1)
                ve.wait_ge(fing_in, 16)
                for t in range(NT):
                    ve.wait_ge(sum_ready, NT * n + t + 1)
                    nc.vector.tensor_tensor(x_res[:, t, cols], out_rows[:, t, cols], fin_g[:, cols], ALU.mult
                                            ).then_inc(gained, 1)
            ve.wait_ge(sq_ready, 8)
            nc.vector.tensor_reduce(ssq_f[:, :], ssq_o[:, :, :], axis=mybir.AxisListType.X, op=ALU.add
                                    ).then_inc(ssq_ready, 1)
            ve.wait_ge(rstd_ready, 3)
            ve.wait_ge(gained, NT * 4)
            for t, half in ((0, 0), (0, 1), (1, 1)):
                cols = slice(D // 2 * half, D // 2 * (half + 1))
                nc.vector.tensor_scalar(x_res[:, t, cols], x_res[:, t, cols], rstd[:, 2, t:t + 1], None, ALU.mult
                                        ).then_inc(normed, 1)

        @block.tensor
        def _(pe):
            mm = nc.tensor.matmul

            def transpose(dst, src, n=P):
                return nc.tensor.transpose(dst, src, ident[0:n, 0:n])

            def banks_free(c):
                kind = KINDS[c.base - 2]
                if kind in "qi":
                    pe.wait_ge(act_evac, c.of(lambda v: acts_before(v - 1)))
                if kind in "qzP":
                    pe.wait_ge(dve_evac, c.of(lambda v: dves_before(v - 1)))
                if kind == "g":
                    pe.wait_ge(tanh_ready, c.of(lambda v: tanhs_before(v - 1)))
                if kind == "o":
                    pe.wait_ge(sum_ready, NT * (c.base - 2 - 42))

            def product(g, c, j, n_pieces, hi_t, lo_t):
                s = g.base % RING
                pe.wait_ge(lo_ready, g.of(lambda v: v + 1))
                wh, wl = (w[:, s, :].rearrange("p (k n) -> p k n", k=2) for w in (w_hi, w_lo))
                b0 = 2 * (c.base % 2)
                for e in range(2):
                    kt = 2 * j + e
                    first, last = kt == 0, kt == 2 * n_pieces - 1
                    for t in range(NT):
                        xh, xl = hi_t[:, kt, t * P:(t + 1) * P], lo_t[:, kt, t * P:(t + 1) * P]
                        acc = bank[b0 + t][:, :]
                        mm(acc, xh, wh[:, e, :], start=first, stop=False)
                        mm(acc, xh, wl[:, e, :], start=False, stop=False)
                        ins = mm(acc, xl, wh[:, e, :], start=False, stop=last)
                ins.then_inc(used, 1)

            def attend(k, br, m):
                a = pair(br, m)
                if k == 0:
                    pe.wait_ge(rows_ready, a.of(lambda n: 2 * n + 2))
                    wait(pe, pT1_copied, a.of(lambda n: n))
                    for e in range(2):
                        for t in range(NT):
                            ins = transpose(bank[7][:, (2 * e + t) * P:(2 * e + t + 1) * P],
                                            rows[:, t, e * P:(e + 1) * P])
                    ins.then_inc(qkT_ready, 1)
                if k == 1:
                    pe.wait_ge(qkT_copied, a.of(lambda n: 2 * n + 2))
                    wait(pe, o_ready, a.of(lambda n: n))
                    for t in (1, 0):
                        for h in range(2):
                            r = slice(HD * h, HD * (h + 1))
                            cols = t_of(t)
                            ins = mm(bank[4 + h][:, cols], qkT[r, t * P:(t + 1) * P],
                                     qkT[r, 2 * P:2 * P + cols.stop - cols.start], start=True, stop=True)
                    ins.then_inc(scored, 1)
                if k == 4:
                    for h in range(2):
                        pe.wait_ge(exp_ready, a.of(lambda n: 5 * n + 2 * h + 2))
                        for blk in range(3):
                            ins = transpose(bank[6 + h][:, blk * P:(blk + 1) * P],
                                            scores[:, h, blk * P:(blk + 1) * P])
                        ins.then_inc(pT_ready, 1)
                if k == 5:
                    pe.wait_ge(pT0_copied, a.of(lambda n: n + 1))
                    pe.wait_ge(pT1_copied, a.of(lambda n: n + 1))
                    for h in range(2):
                        o1 = bank[4][:, P + HD * h:P + HD * (h + 1)]
                        mm(o1, probsT[:, h, 0:P], v_cols(br, m, 0, h), start=True, stop=False)
                        mm(o1, probsT[:, h, P:2 * P], v_cols(br, m, 1, h), start=False, stop=True)
                        ins = mm(bank[4][:, HD * h:HD * (h + 1)], probsT[:, h, 2 * P:3 * P],
                                 v_cols(br, m, 0, h), start=True, stop=True)
                    ins.then_inc(pv_ready, 1)

            def transpose_rows(k, src, dst_bank, ready):
                for e in range(2):
                    for t in range(NT):
                        ins = transpose(dst_bank[:, e * SEQ + t * P:e * SEQ + (t + 1) * P],
                                        src[:, t, (2 * k + e) * P:(2 * k + e + 1) * P])
                ins.then_inc(ready, 1)

            pe.wait_ge(ident_ready, 1)
            with pe.Fori(0, WARM_UP // 8):
                for _ in range(8):
                    transpose(bank[3][:, 0:P], ident[:, :])
            pe.wait_ge(lng_in, 16)
            transpose(bank[0][:, 0:KT], lng_r[:, :], KT).then_inc(lngT_ready, 1)

            def h_group(k):
                pe.wait_ge(x_normed, NT * (k // 2 + 1))
                transpose_rows(k, x_rows, bank[4 + k % 4], hT_ready)

            h_group(0)
            h_group(1)
            pe.wait_ge(lngT_copied, 1)
            for j in range(8):
                pe.wait_ge(hT_lo, 2 * (j + 1))
                product(Idx(j), Idx(0), j, 8, h_hi, h_lo)
                if j == 0:
                    h_group(2)
                    h_group(3)
                if j < 4:
                    h_group(4 + j)
            for j in range(8):
                product(Idx(FIRST[1] + j), Idx(1), j, 8, h_hi, h_lo)
                if j == 4:
                    pe.wait_ge(ckv_normed, 2)
                    for c in range(2):
                        for t in range(NT):
                            ins = transpose(bank[7][:, c * SEQ + t * P:c * SEQ + (t + 1) * P],
                                            ckv[:, t, c * P:(c + 1) * P])
                    ins.then_inc(ckvT_ready, 1)
            banks_free(Idx(2))
            for j in range(4):
                s = (FIRST[2] + j) % RING
                pe.wait_ge(lo_ready, FIRST[2] + j + 1)
                wh, wl = (w[:, s, 0:288].rearrange("p (k n) -> p k n", k=4) for w in (w_hi, w_lo))
                for e in range(4):
                    kt = 4 * j + e
                    acc = bank[0][0:72, 0:SEQ]
                    mm(acc, wh[:, e, :], h_hi[:, kt, :], start=kt == 0, stop=False)
                    mm(acc, wh[:, e, :], h_lo[:, kt, :], start=False, stop=False)
                    ins = mm(acc, wl[:, e, :], h_hi[:, kt, :], start=False, stop=kt == KT - 1)
                ins.then_inc(used, 1)
            banks_free(Idx(3))
            for j in range(8):
                product(Idx(FIRST[3] + j), Idx(3), j, 8, h_hi, h_lo)
                if j == 0:
                    pe.wait_ge(act_evac, 3)
                    pe.wait_ge(dve_evac, 2)
                    for k in range(2):
                        transpose_rows(k, v_b, bank[4 + k], iqT_ready)
                    for t in range(NT):
                        ins = nc.tensor.transpose(bank[6][:, t * IH:(t + 1) * IH], iwT[:, t * P:(t + 1) * P],
                                                  ident[HD:HD + IH, HD:HD + IH])
                    ins.then_inc(iqT_ready, 1)
                if 3 <= j <= 6:
                    for h in (2 * (j - 3), 2 * (j - 3) + 1):
                        pe.wait_ge(iqT_copied, 3)
                        wait(pe, idx_relu, h - 3)
                        r = slice(HD * (h % 2), HD * (h % 2 + 1))
                        dst = bank[4 + h % 4]
                        mm(dst[:, 0:256], iqT[r, h // 2, P:2 * P], ikT[r, :], start=True, stop=True)
                        mm(dst[:, 256:384], iqT[r, h // 2, 0:P], ikT[r, 0:P], start=True, stop=True
                           ).then_inc(idx_mm, 1)
            banks_free(Idx(4))
            for j in range(8):
                product(Idx(FIRST[4] + j), Idx(4), j, 8, h_hi, h_lo)
            pe.wait_ge(idx_relu, IH)
            pe.wait_ge(ckvT_copied, 1)

            def pair_a_chunk(m, g, c):
                banks_free(c)
                for j in range(8):
                    product(g + j, c, j, 8, h_hi, h_lo)
                    if j == 0:
                        pe.wait_ge(uk_in, m.of(lambda n: 16 * n + 16))
                        wait(pe, pT0_copied, m.of(lambda n: n))
                        for k in range(2):
                            ins = transpose(bank[6][:, k * P:(k + 1) * P], uk[:, k * P:(k + 1) * P])
                        ins.then_inc(ukT_ready, 1)
                    attend(j - 1, 0, m)
                    if j == 3:
                        pe.wait_ge(ukT_copied, m.of(lambda n: n + 1))
                        pe.wait_ge(uv_in, m.of(lambda n: 32 * n + 32))
                        for t in range(NT):
                            for k in range(2):
                                ins = mm(bank[7][:, t * 2 * P:(t + 1) * 2 * P], ckvT[:, k, t * P:(t + 1) * P],
                                         ukv[:, k, :], start=k == 0, stop=k == 1)
                        ins.then_inc(kv_ready, 1)
                    if j == 4:
                        pe.wait_ge(kv_copied, m.of(lambda n: 2 * n + 2))

            for u in range(2):
                pair_a_chunk(Idx(u), Idx(FIRST[5 + u]), Idx(5 + u))
            with pe.Fori(0, 3) as i:
                for u in range(2):
                    pair_a_chunk(Idx(2 + u, 2, i), Idx(FIRST[7 + u], 16, i), Idx(7 + u, 2, i))
            for b in range(3):
                c0, g0 = 13 + BR * b, FIRST[13 + BR * b]
                for u in range(2):
                    banks_free(Idx(c0 + u))
                    for j in range(8):
                        product(Idx(g0 + 8 * u + j), Idx(c0 + u), j, 8, h_hi, h_lo)
                        if b < 2:
                            attend(j - 1, b + 1, Idx(u))
                banks_free(Idx(c0 + 2))
                for j in range(8):
                    product(Idx(g0 + 16 + j), Idx(c0 + 2), j, 8, h_hi, h_lo)
                    if 1 <= j <= 4:
                        k = j - 1
                        pe.wait_ge(dve_evac, dves_before(c0 + 1 + k // 2))
                        if k == 0 and b < 2:
                            pe.wait_ge(o_ready, 8 * (b + 1) + 2)
                        transpose_rows(k, act[:, :, BW * b:BW * (b + 1)], bank[4 + k], yT_ready)
                pe.wait_ge(yT_lo, 4 * (b + 1))
                with pe.Fori(0, 3) as i:
                    banks_free(Idx(c0 + 3, 2, i))
                    for j in range(12):
                        if j < 4:
                            product(Idx(g0 + 24 + j, 12, i), Idx(c0 + 3, 2, i), j, 4, y_hi, y_lo)
                        else:
                            if j == 4:
                                banks_free(Idx(c0 + 4, 2, i))
                            product(Idx(g0 + 24 + j, 12, i), Idx(c0 + 4, 2, i), j - 4, 8, h_hi, h_lo)
                        if b < 2:
                            attend(j, b + 1, Idx(2, 2, i))
                            attend(j - 5, b + 1, Idx(3, 2, i))
                banks_free(Idx(c0 + 9))
                for j in range(4):
                    product(Idx(g0 + 60 + j), Idx(c0 + 9), j, 4, y_hi, y_lo)
                    if b == 2 and j < 3:
                        for e in range(2):
                            k = 2 * j + e
                            pe.wait_ge(dve_evac, dves_before(c0 + 9))
                            wait(pe, mT_lo, k - 3)
                            transpose_rows(k, merged, bank[4 + k % 4], mT_ready)
            for n in range(4):
                banks_free(Idx(43 + n))
                for j in range(8):
                    if n == 0:
                        pe.wait_ge(mT_lo, j + 1)
                    product(Idx(FIRST[43 + n] + j), Idx(43 + n), j, 8, h_hi, h_lo)
                    if n == 0 and j == 1:
                        pe.wait_ge(dve_evac, dves_before(43))
                        for k in (6, 7):
                            wait(pe, mT_lo, k - 3)
                            transpose_rows(k, merged, bank[4 + k % 4], mT_ready)


_INS = ["x", "ln_g", "w_in", "ckv_g", "w_uk", "w_uv", "sink", "c_rel_bias", "t5_bias", "w_pa", "w_pb", "w_pc",
        "w_o", "final_g"]


def kernel(**inputs):
    import numpy as _np
    import concourse.bacc as _bacc
    from concourse import mybir as _mybir
    from concourse.bass_utils import run_bass_kernel_spmd as _run

    nc = _bacc.Bacc("TRN2", target_bir_lowering=False, num_devices=1)
    arrays, args = {}, []
    for name in _INS:
        a = _np.ascontiguousarray(inputs[name])
        arrays[f"in_{name}_dram"] = a
        args.append(nc.dram_tensor(f"in_{name}_dram", a.shape, _mybir.dt.from_np(a.dtype), kind="ExternalInput").ap())
    args.append(nc.dram_tensor("out_dram", (1, SEQ, D), _mybir.dt.float32, kind="ExternalOutput").ap())
    hybrid_trunk(nc, *args)
    r = _run(nc, [arrays], core_ids=[0])
    return r.results[0]["out_dram"]
```
